# Optimizing a Trainium2 kernel written in Bass

```python
import math
import jax
import jax.numpy as jnp
from jax import lax
import numpy as np

D_MODEL = 2048
BATCH = 1
SEQ = 256
DEPTH = 2

GRID_W = 64
CTX_LEN = 256
EPS = 1e-6
HEAD_DIM = 128
A_WIDTH = D_MODEL // 2
A_CH = 128
A_GROUPS = A_WIDTH // A_CH
CHUNK = 128
B_HEADS = (D_MODEL // 2) // HEAD_DIM
B_KV_HEADS = max(1, B_HEADS // 4)
B_GROUP = B_HEADS // B_KV_HEADS
B_Q_W = B_HEADS * HEAD_DIM
B_KV_W = B_KV_HEADS * HEAD_DIM
Q_BLOCK = 128
ROPE_THETA = 10000.0
AXIS_DIM = HEAD_DIM // 2
AB_SPLITS = (A_WIDTH, 2 * A_WIDTH, 3 * A_WIDTH, 3 * A_WIDTH + B_Q_W,
             3 * A_WIDTH + B_Q_W + B_KV_W, 3 * A_WIDTH + B_Q_W + 2 * B_KV_W)
AB_IN_W = 3 * A_WIDTH + 2 * B_Q_W + 2 * B_KV_W
AB_OUT_W = A_WIDTH + B_Q_W
DN_K_HEADS = D_MODEL // HEAD_DIM
DN_V_HEADS = 2 * DN_K_HEADS
DN_K_W = DN_K_HEADS * HEAD_DIM
DN_V_W = DN_V_HEADS * HEAD_DIM
DN_QKV_W = 2 * DN_K_W + DN_V_W
DN_IN_W = DN_QKV_W + DN_V_W + 4 * DN_V_HEADS
DN_CHUNK = 64
CONV_K = 5

kernel_name = 'hybrid_prefix_gmlp_gqa_gdn'

F32 = jnp.float32

def rms_norm(x, w):
    xf = x.astype(F32)
    y = xf * lax.rsqrt(jnp.mean(xf * xf, axis=-1, keepdims=True) + EPS)
    return (y * w.astype(F32)).astype(x.dtype)

def l2_norm(x):
    xf = x.astype(F32)
    return (xf * lax.rsqrt(jnp.sum(xf * xf, axis=-1, keepdims=True) + EPS)).astype(x.dtype)

def ada_mod(cond, w, b):
    m = jax.nn.silu(cond) @ w + b
    return jnp.split(m[..., None, :], 3, axis=-1)

def axial_rope_tables(rows):
    row = jnp.repeat(jnp.arange(rows), GRID_W).astype(F32)
    col = jnp.tile(jnp.arange(GRID_W), rows).astype(F32)
    freqs = ROPE_THETA ** (-jnp.arange(0, AXIS_DIM, 2, dtype=F32) / AXIS_DIM)
    ang_r = row[:, None] * freqs[None, :]
    ang_c = col[:, None] * freqs[None, :]
    ang = jnp.concatenate([ang_r, ang_r, ang_c, ang_c], axis=-1)
    return jnp.cos(ang), jnp.sin(ang)

def apply_rope(x, cos, sin):
    xr = x.reshape(x.shape[:-1] + (2, 2, AXIS_DIM // 2))
    rot = jnp.stack([-xr[..., 1, :], xr[..., 0, :]], axis=-2).reshape(x.shape)
    return x * cos[None, :, None, :].astype(x.dtype) + rot * sin[None, :, None, :].astype(x.dtype)

def block_attention(q, k, v):
    bn, lq = q.shape[:2]
    nb = lq // Q_BLOCK
    qb = q.reshape(bn, nb, Q_BLOCK, B_KV_HEADS, B_GROUP, HEAD_DIM).transpose(1, 0, 2, 3, 4, 5)

    def attend(qblk):
        s = jnp.einsum('bqkgd,bskd->bkgqs', qblk, k).astype(F32) * (HEAD_DIM ** -0.5)
        p = jax.nn.softmax(s, axis=-1).astype(v.dtype)
        return jnp.einsum('bkgqs,bskd->bqkgd', p, v)

    o = lax.map(attend, qb)
    return o.transpose(1, 0, 2, 3, 4, 5).reshape(bn, lq, B_Q_W)

def chunk_sgu(u, v, w_s, b_s):
    bn, l, _ = u.shape
    vg = v.astype(F32).reshape(bn, l // CHUNK, CHUNK, A_GROUPS, A_CH)
    mu = jnp.mean(vg, axis=-1, keepdims=True)
    var = jnp.mean(jnp.square(vg - mu), axis=-1, keepdims=True)
    vn = ((vg - mu) * lax.rsqrt(var + 1e-5)).astype(u.dtype)
    mixed = jnp.einsum('gij,bnjgc->bnigc', w_s, vn) + b_s.T[None, None, :, :, None]
    return u * mixed.reshape(bn, l, A_WIDTH)

def ab_project(h, w_in, qn_w, kn_w):
    bn, l, _ = h.shape
    u, v, ga, q, k, vv, gb = jnp.split(h @ w_in, AB_SPLITS, axis=-1)
    q = rms_norm(q.reshape(bn, l, B_HEADS, HEAD_DIM), qn_w)
    k = rms_norm(k.reshape(bn, l, B_KV_HEADS, HEAD_DIM), kn_w)
    vv = vv.reshape(bn, l, B_KV_HEADS, HEAD_DIM)
    return u, v, ga, q, k, vv, gb

def ab_mixer(h_lat, h_ctx, w_in, w_out, w_s, b_s, qn_w, kn_w, cos, sin, need_ctx_out):
    lu, lv, lga, lq, lk, lvv, lgb = ab_project(h_lat, w_in, qn_w, kn_w)
    cu, cv, cga, cq, ck, cvv, cgb = ab_project(h_ctx, w_in, qn_w, kn_w)
    lq = apply_rope(lq, cos, sin)
    lk = apply_rope(lk, cos, sin)
    k_all = jnp.concatenate([ck, lk], axis=1)
    v_all = jnp.concatenate([cvv, lvv], axis=1)

    def merge(u, v, ga, attn_o, gb):
        a_out = chunk_sgu(u, v, w_s, b_s) * jax.nn.silu(ga)
        b_out = attn_o * jax.nn.silu(gb)
        return jnp.concatenate([a_out, b_out], axis=-1) @ w_out

    lat = merge(lu, lv, lga, block_attention(lq, k_all, v_all), lgb)
    ctx_out = merge(cu, cv, cga, block_attention(cq, ck, cvv), cgb) if need_ctx_out else None
    return lat, ctx_out

def centred_conv(x, w):
    return lax.conv_general_dilated(
        x, w.astype(x.dtype)[:, None, :], window_strides=(1,),
        padding=[(CONV_K // 2, CONV_K // 2)], dimension_numbers=('NWC', 'WIO', 'NWC'),
        feature_group_count=x.shape[-1])

def gated_delta_rule(q, k, v, g, beta, state):
    bn, l, h, _ = q.shape
    dv = v.shape[-1]
    n = l // DN_CHUNK

    def chunks(t):
        return t.astype(F32).reshape(bn, n, DN_CHUNK, h, -1).transpose(1, 0, 3, 2, 4)

    q, k, v = chunks(q), chunks(k), chunks(v)
    g = chunks(g[..., None])[..., 0]
    beta = chunks(beta[..., None])[..., 0]
    gc = jnp.cumsum(g, axis=-1)
    tril = jnp.tril(jnp.ones((DN_CHUNK, DN_CHUNK), dtype=bool))
    strict = jnp.tril(jnp.ones((DN_CHUNK, DN_CHUNK), dtype=bool), -1)
    decay = jnp.exp(jnp.where(tril, gc[..., :, None] - gc[..., None, :], -jnp.inf))
    kb = k * beta[..., None]
    lmat = jnp.where(strict, jnp.einsum('nbhid,nbhjd->nbhij', kb, k) * decay, 0.0)
    tmat = lmat + jnp.eye(DN_CHUNK, dtype=F32)
    rhs = jnp.concatenate([v * beta[..., None], kb * jnp.exp(gc)[..., None]], axis=-1)
    sol = lax.linalg.triangular_solve(tmat, rhs, left_side=True, lower=True, unit_diagonal=True)
    u_c, w_c = sol[..., :dv], sol[..., dv:]
    attn = jnp.einsum('nbhid,nbhjd->nbhij', q, k) * decay
    qg = q * jnp.exp(gc)[..., None]
    kd = k * jnp.exp(gc[..., -1:] - gc)[..., None]
    gl = jnp.exp(gc[..., -1])[..., None, None]

    def step(s, xs):
        attn_n, u_n, w_n, qg_n, kd_n, gl_n = xs
        v_new = u_n - jnp.einsum('bhcd,bhde->bhce', w_n, s)
        o = jnp.einsum('bhcd,bhde->bhce', qg_n, s) + jnp.einsum('bhij,bhje->bhie', attn_n, v_new)
        s = s * gl_n + jnp.einsum('bhcd,bhce->bhde', kd_n, v_new)
        return s, o

    state, o = lax.scan(step, state.astype(F32), (attn, u_c, w_c, qg, kd, gl))
    return o.transpose(1, 0, 3, 2, 4).reshape(bn, l, h, dv), state

def dn_prepare(h, w_in, conv_w, a_log, dt_bias):
    bn, l, _ = h.shape
    qkv, z, ba = jnp.split(h @ w_in, (DN_QKV_W, DN_QKV_W + DN_V_W), axis=-1)
    qkv = jax.nn.silu(centred_conv(qkv, conv_w))
    q, k, v = jnp.split(qkv, (DN_K_W, 2 * DN_K_W), axis=-1)
    rep = DN_V_HEADS // DN_K_HEADS
    q = l2_norm(q.reshape(bn, l, DN_K_HEADS, HEAD_DIM)) * (HEAD_DIM ** -0.5)
    k = l2_norm(k.reshape(bn, l, DN_K_HEADS, HEAD_DIM))
    q = jnp.repeat(q, rep, axis=2)
    k = jnp.repeat(k, rep, axis=2)
    v = v.reshape(bn, l, DN_V_HEADS, HEAD_DIM)
    ba = ba.astype(F32).reshape(bn, l, 2, 2, DN_V_HEADS)
    beta = jax.nn.sigmoid(ba[:, :, :, 0])
    g = -jnp.exp(a_log.astype(F32)) * jax.nn.softplus(ba[:, :, :, 1] + dt_bias.astype(F32))
    return q, k, v, z, beta, g

def dn_bidir(q, k, v, beta, g, s_fwd, s_bwd):
    o_f, s_f = gated_delta_rule(q, k, v, g[:, :, 0], beta[:, :, 0], s_fwd)
    fl = lambda t: jnp.flip(t, axis=1)
    o_b, s_b = gated_delta_rule(fl(q), fl(k), fl(v), fl(g[:, :, 1]), fl(beta[:, :, 1]), s_bwd)
    return o_f + fl(o_b), s_f, s_b

def dn_out(o, z, norm_w, w_out):
    bn, l, _ = z.shape
    zh = z.reshape(bn, l, DN_V_HEADS, HEAD_DIM)
    y = rms_norm(o.astype(z.dtype), norm_w) * jax.nn.silu(zh)
    return y.reshape(bn, l, DN_V_W) @ w_out

def dn_mixer(h_lat, h_ctx, w_in, conv_w, a_log, dt_bias, norm_w, w_out, need_ctx_out):
    cq, ck, cv, cz, cbeta, cg = dn_prepare(h_ctx, w_in, conv_w, a_log, dt_bias)
    zero = jnp.zeros((h_ctx.shape[0], DN_V_HEADS, HEAD_DIM, HEAD_DIM), F32)
    co, cs_f, cs_b = dn_bidir(cq, ck, cv, cbeta, cg, zero, zero)
    lq, lk, lv, lz, lbeta, lg = dn_prepare(h_lat, w_in, conv_w, a_log, dt_bias)
    lo, _, _ = dn_bidir(lq, lk, lv, lbeta, lg, cs_f, cs_b)
    lat = dn_out(lo, lz, norm_w, w_out)
    ctx_out = dn_out(co, cz, norm_w, w_out) if need_ctx_out else None
    return lat, ctx_out

def setup_inputs(seed: int = 0) -> dict:
    key = jax.random.key(seed)
    ks = jax.random.split(key, 20)
    n_even = (DEPTH + 1) // 2
    n_odd = DEPTH // 2

    def nrm(k, shape, scale):
        return jax.random.normal(k, shape, F32) * scale

    dt = jnp.exp(jax.random.uniform(ks[16], (n_odd, 2, DN_V_HEADS), F32,
                                    math.log(1e-3), math.log(1e-1)))
    return {
        'x': nrm(ks[0], (BATCH, SEQ, D_MODEL), 1.0),
        'c': nrm(ks[1], (BATCH, D_MODEL), 1.0),
        'ctx': nrm(ks[2], (BATCH, CTX_LEN, D_MODEL), 1.0),
        'c_ctx': nrm(ks[3], (D_MODEL,), 1.0),
        'norm_w': 1.0 + nrm(ks[4], (DEPTH, D_MODEL), 0.02),
        'ada_w': nrm(ks[5], (DEPTH, D_MODEL, 3 * D_MODEL), 0.5 * D_MODEL ** -0.5),
        'ada_b': nrm(ks[6], (DEPTH, 3 * D_MODEL), 0.02),
        'ab_w_in': nrm(ks[7], (n_even, D_MODEL, AB_IN_W), D_MODEL ** -0.5),
        'ab_w_out': nrm(ks[8], (n_even, AB_OUT_W, D_MODEL), AB_OUT_W ** -0.5),
        'sgu_w': nrm(ks[9], (n_even, A_GROUPS, CHUNK, CHUNK), CHUNK ** -0.5),
        'sgu_b': nrm(ks[10], (n_even, A_GROUPS, CHUNK), 0.02),
        'q_norm_w': 1.0 + nrm(ks[11], (n_even, HEAD_DIM), 0.02),
        'k_norm_w': 1.0 + nrm(ks[12], (n_even, HEAD_DIM), 0.02),
        'dn_w_in': nrm(ks[13], (n_odd, D_MODEL, DN_IN_W), D_MODEL ** -0.5),
        'dn_conv_w': nrm(ks[14], (n_odd, CONV_K, DN_QKV_W), CONV_K ** -0.5),
        'dn_a_log': jnp.log(jax.random.uniform(ks[15], (n_odd, 2, DN_V_HEADS), F32, 1.0, 16.0)),
        'dn_dt_bias': dt + jnp.log(-jnp.expm1(-dt)),
        'dn_norm_w': 1.0 + nrm(ks[17], (n_odd, HEAD_DIM), 0.02),
        'dn_w_out': nrm(ks[18], (n_odd, DN_V_W, D_MODEL), DN_V_W ** -0.5),
        'final_norm_w': 1.0 + nrm(ks[19], (D_MODEL,), 0.02),
    }

def reference(x, c, ctx, c_ctx, norm_w, ada_w, ada_b, ab_w_in, ab_w_out, sgu_w, sgu_b,
              q_norm_w, k_norm_w, dn_w_in, dn_conv_w, dn_a_log, dn_dt_bias, dn_norm_w,
              dn_w_out, final_norm_w):
    rows = x.shape[1] // GRID_W
    cos, sin = axial_rope_tables(rows)
    for i in range(DEPTH):
        need_ctx_out = i < DEPTH - 1
        shift, scale, gate = ada_mod(c, ada_w[i], ada_b[i])
        c_shift, c_scale, c_gate = ada_mod(c_ctx, ada_w[i], ada_b[i])
        h = rms_norm(x, norm_w[i]) * (1.0 + scale) + shift
        hc = rms_norm(ctx, norm_w[i]) * (1.0 + c_scale) + c_shift
        j = i // 2
        if i % 2 == 0:
            o, oc = ab_mixer(h, hc, ab_w_in[j], ab_w_out[j], sgu_w[j], sgu_b[j],
                             q_norm_w[j], k_norm_w[j], cos, sin, need_ctx_out)
        else:
            o, oc = dn_mixer(h, hc, dn_w_in[j], dn_conv_w[j], dn_a_log[j], dn_dt_bias[j],
                             dn_norm_w[j], dn_w_out[j], need_ctx_out)
        x = x + gate * o
        if need_ctx_out:
            ctx = ctx + c_gate * oc
    return rms_norm(x, final_norm_w)


_drawn_inputs = setup_inputs


def setup_inputs(seed=0):
    import zlib

    import numpy as np

    out = dict(_drawn_inputs(seed))
    spreads = {}
    factors = {'norm_w': 7.126,
     'ada_b': 2.78,
     'sgu_b': 8.0,
     'q_norm_w': 8.0,
     'k_norm_w': 8.0,
     'dn_norm_w': 8.0,
     'final_norm_w': 2.912}
    for name, (base, spread) in spreads.items():
        noise = np.random.default_rng([zlib.crc32(name.encode()), seed]).standard_normal(out[name].shape)
        drawn = base * np.exp(spread * noise) if base else spread * noise
        out[name] = jnp.asarray(drawn.astype(out[name].dtype))
    for name, factor in factors.items():
        out[name] = (out[name] * factor).astype(out[name].dtype)
    return out
```

```python
from contextlib import ExitStack

import numpy as np

import concourse.bass as bass
from concourse import mybir

F32 = mybir.dt.float32
F32R = mybir.dt.float32r
U8 = mybir.dt.uint8
ALU = mybir.AluOpType
ACT = mybir.ActivationFunctionType
AX = mybir.AxisListType.X

P = 128
D = 2048
KT = D // P
SEG = 256
T = 2 * SEG
NT = T // P
HD = 128
HALF = 8
AW = D // 2
GROUPS = AW // P
QH = (D // 2) // HD
KVH = QH // 4
KH = D // HD
VH = 2 * KH
LEVELS = 7
NMASK = (3 * LEVELS + 1) * P
EPS = 1e-6
SGU_EPS = 1e-5
SCALE = HD ** -0.5

RAW = 4
PHASES = [("ada0", 6 * KT), ("kv", 4 * KVH), ("mix", 10 * GROUPS), ("out0", 2 * KT),
          ("ada1", 6 * KT), ("ba", 2), ("delta", 12 * KH), ("out1", 4 * KT)]
FIRST = {}
_n = 0
for _name, _count in PHASES:
    FIRST[_name] = _n
    _n += _count

SMALL = [("cond", 2 * KT), ("ada_b", 2 * 3 * KT), ("norm_w", 2 * KT), ("final_w", KT), ("q_w", 1), ("k_w", 1),
         ("o_w", 1), ("conv_w", KH * 4 * 5), ("dt_bias", 2 * VH), ("a_log", 2 * VH), ("ident", P), ("tri", 2 * P)]
MIXC = [("ws", GROUPS * P), ("cos", SEG), ("sin", SEG), ("rot", P)]


def offsets(table):
    out, n = {}, 0
    for name, width in table:
        out[name] = (n, n + width)
        n += width
    return out, n


SO, NSMALL = offsets(SMALL)
MO, NMIX = offsets(MIXC)


class Chain:

    def __init__(self, eng, sem):
        self.eng, self.sem, self.base, self.n, self.per, self.i = eng, sem, 0, 0, 0, 0

    def start(self, i, per):
        self.base, self.n, self.per, self.i = self.base + self.n, 0, per, i

    def end(self, trips):
        assert self.n == self.per, f"{self.sem} steps in a trip: {self.n}, given {self.per}"
        self.base, self.n, self.per, self.i = self.base + trips * self.per, 0, 0, 0

    def link(self, ins):
        ins.then_inc(self.sem, 1)
        self.n += 1
        self.eng.wait_ge(self.sem, self.i * self.per + (self.base + self.n))


def build(nc, xT, w_ada, w_in0, w_out0, w_in1, w_out1, small, mixc, sgu_b, masks, out, keep_x1):
    ctx = ExitStack()
    with ctx:
        def sb(name, shape, dt=F32):
            return ctx.enter_context(nc.sbuf_tensor(name, shape, dt))

        used = {}

        def sem(name):
            if name not in used:
                used[name] = ctx.enter_context(nc.semaphore(name))
            return used[name]

        hh = sb("hh", [P, KT * T], F32R)
        hl = sb("hl", [P, KT * T], F32R)
        mbuf = sb("mbuf", [P, KT * T])
        raw = sb("raw", [P, RAW, HALF * P])
        wh = sb("wh", [P, 2, HALF * P], F32R)
        wl = sb("wl", [P, 2, HALF * P], F32R)
        sm = sb("sm", [P, NSMALL])
        mk = sb("mk", [P, NMASK], U8)
        ones = sb("ones", [P, P])
        mod = sb("mod", [P, 3 * KT, 2])
        affa = sb("affa", [P, KT, 2])
        silc = sb("silc", [P, 2 * KT])
        eps = sb("eps", [P, 2])

        def smc(name):
            return sm[:, SO[name][0]:SO[name][1]]

        scope = ExitStack()
        count = [0]

        def cut(width, dt=F32):
            count[0] += 1
            return scope.enter_context(nc.sbuf_tensor(f"scratch{count[0]}", [P, width], dt))[:, :]

        ident = smc("ident")
        xv = mbuf[:, :].rearrange("p (k t) -> p k t", t=T)
        hhv = hh[:, :].rearrange("p (k t) -> p k t", t=T)
        hlv = hl[:, :].rearrange("p (k t) -> p k t", t=T)
        hhy = hh[:, :].rearrange("p (k t) -> p k t", t=SEG)
        hly = hl[:, :].rearrange("p (k t) -> p k t", t=SEG)
        yv = mbuf[:, :].rearrange("p (k t) -> p k t", t=SEG)
        wins = [raw[:, s, :].rearrange("p (k n) -> p k n", n=P) for s in range(RAW)]
        whv = [wh[:, s, :].rearrange("p (k n) -> p k n", n=P) for s in range(2)]
        wlv = [wl[:, s, :].rearrange("p (k n) -> p k n", n=P) for s in range(2)]

        masks_in = cut(NMASK)
        n_sq = [cut(T), cut(T)]
        n_rinv = cut(T)
        n_full = [cut(T), cut(T)]
        n_t = [cut(T), cut(T)]

        scope.close()
        mc = cut(NMIX)
        sgub = cut(GROUPS * P)
        kTa = cut(KVH * T)
        vva = cut(KVH * T)
        a_raw = cut(T)
        a_sq = cut(T)
        a_rinv = cut(T)
        a_q = cut(T)
        a_rot = cut(SEG)
        a_vT = cut(T)
        a_vn = cut(T)
        a_vsq = cut(T)
        a_ug = cut(T)
        a_ga = cut(T)
        a_gb = cut(T)
        a_p = cut(2 * SEG + 2 * T)
        a_pt = cut(6 * SEG)
        a_col = cut(40)
        scope.close()
        xres = cut(KT * T).rearrange("p (k t) -> p k t", t=T)

        scope.close()
        cols = cut(7 * 8 * VH)
        colv = cols.rearrange("p (r h) -> p r h", h=VH)
        ck = cut(7 * 16)
        acc = [cut(T), cut(T)]
        kT = cut(T)
        qT = cut(SEG)
        vtok = [cut(T), cut(T)]
        ktok = cut(T)
        d_sq = cut(T)
        KK = d_sq
        d_rinv = cut(T)
        attn = [cut(T), cut(T)]
        identr = cut(P, F32R)
        twice = cut(P, F32R)
        PI = [cut(T, F32R) for _ in range(NT)]

        def shared(widths_a, dt_a, widths_b, dt_b):
            outer, base = scope, ExitStack()
            names = []
            for widths, dt in ((widths_a, dt_a), (widths_b, dt_b)):
                part = ExitStack()
                got = []
                for w in widths:
                    count[0] += 1
                    got.append(part.enter_context(nc.sbuf_tensor(f"scratch{count[0]}", [P, w], dt))[:, :])
                names.append(got)
                part.close()
            outer.enter_context(nc.sbuf_tensor(f"room{count[0]}", [P, max(sum(widths_a), sum(widths_b))], F32))
            return names

        CT, SR = shared([T] * 4, F32, [T] * 4, F32)
        CR, PF = shared([T] * 4, F32R, [T] * 4, F32)
        M, VN = shared([T] * 4, F32R, [T] * 4, F32)
        X1, QG = shared([T] * 4, F32R, [T] * 2, F32)
        b_fm, b_t = kT, [SR[n][:, 0:SEG] for n in range(4)] + [VN[n][:, 0:SEG] for n in range(2)]
        scope.close()
        x1 = cut(KT * SEG).rearrange("p (k t) -> p k t", t=SEG)
        f_sq = [cut(SEG), cut(SEG)]
        f_rinv = cut(SEG)
        f_out = [cut(SEG), cut(SEG)]
        scope.close()

        G_, GC, NBETA, BETA, BEKD, NEGC, GL = range(7)

        def col(kind, c, u):
            n = kind * 16 + c * 4 + u
            return ck[:, n:n + 1]

        def col4(kind, c, width=P):
            n = kind * 16 + c * 4
            return ck[:, n:n + 4].rearrange("p (u o) -> p u o", o=1).to_broadcast([P, 4, width])

        def u4(ap):
            return ap.rearrange("p (u n) -> p u n", n=P)

        def q4(ap):
            return ap.rearrange("p (d v n) -> p d v n", v=2, n=P)

        def over4(ap):
            return ap.rearrange("p (o n) -> p o n", o=1).to_broadcast([P, 4, P])

        pb = [ctx.enter_context(nc.psum_tensor(f"bank{i}", [P, T], F32)) for i in range(8)]

        loaded = [sem(f"loaded{s}") for s in range(RAW)]
        half_done = sem("half_done")
        wh_ready, wl_ready = sem("wh_ready"), sem("wl_ready")
        block = ctx.enter_context(nc.Block())

        def begin(eng, *names):
            for name in names:
                eng.sem_inc(sem(name), 1)

        def load_half(eng, phase, src, i, per, j):
            s = (FIRST[phase] + j) % RAW
            eng.wait_ge(half_done, i * per + (FIRST[phase] + j - RAW + 1))
            eng.dma_start(raw[:, s, :], src).then_inc(loaded[s], 16)

        def slot_loads(phase, i, per, j):
            return i * (per // RAW * 16) + ((FIRST[phase] + j) // RAW + 1) * 16

        def splits(phase):
            n = 0
            for name, count in PHASES:
                if name == phase:
                    return n
                if not name.startswith("ada"):
                    n += count

        def split_hi(eng, phase, i, per, j):
            eng.wait_ge(loaded[(FIRST[phase] + j) % RAW], slot_loads(phase, i, per, j))
            eng.wait_ge(half_done, i * per + (FIRST[phase] + j - 1))
            eng.activation(wh[:, j % 2, :], raw[:, (FIRST[phase] + j) % RAW, :], ACT.Copy).then_inc(wh_ready, 1)

        def lo_count(phase, i, per, j):
            if phase == "delta":
                return i * (per // 2) + ((j // 2 + 1) if j % 2 else (splits(phase) + j // 2 + 1))
            return i * per + (splits(phase) + j + 1 - (6 * KH if phase == "out1" else 0))

        def split_lo(eng, phase, i, per, j):
            eng.wait_ge(wh_ready, i * per + (splits(phase) + j + 1))
            if phase == "delta" and j % 2:
                eng.tensor_tensor(wl[:, j % 2, :], raw[:, (FIRST[phase] + j) % RAW, :],
                                  wh[:, j % 2, :].bitcast(F32), ALU.subtract).then_inc(sem("wl_pool"), 1)
                return
            eng.tensor_tensor(wl[:, j % 2, :], raw[:, (FIRST[phase] + j) % RAW, :], wh[:, j % 2, :].bitcast(F32),
                              ALU.subtract).then_inc(wl_ready, 1)

        def project(eng, phase, i, per, j, ps, moving_h, moving_l, first, last):
            eng.wait_ge(sem("wl_pool") if phase == "delta" and j % 2 else wl_ready, lo_count(phase, i, per, j))
            s = j % 2
            for k in range(HALF):
                eng.matmul(ps, whv[s][:, k, :], moving_h(k), start=first and k == 0, stop=False)
                eng.matmul(ps, whv[s][:, k, :], moving_l(k), start=False, stop=False)
                done = eng.matmul(ps, wlv[s][:, k, :], moving_h(k), start=False, stop=last and k == HALF - 1)
            done.then_inc(half_done, 1)

        def tile(eng, phase, i, per, n, ps, t0=0, t1=T):
            for b in range(2):
                project(eng, phase, i, per, 2 * n + b, ps,
                        lambda k: hhv[:, b * HALF + k, t0:t1], lambda k: hlv[:, b * HALF + k, t0:t1],
                        b == 0, b == 1)

        def tile_done(phase, i, per, n):
            return i * per + (FIRST[phase] + 2 * n + 2)

        @block.sync
        def _(sp):
            sp.dma_start(sm[:, :], small).then_inc(sem("small_in"), 16)
            sp.dma_start(masks_in, masks).then_inc(sem("small_in"), 16)
            sp.dma_start(mbuf[:, :], xT).then_inc(sem("x_in"), 16)

            def ada(layer):
                ph = f"ada{layer}"
                if layer == 0:
                    for j in range(4):
                        sp.dma_start(raw[:, j, :], w_ada[0, j, :, :]).then_inc(loaded[j], 16)
                with sp.Fori(1 - layer, 24) as i:
                    for j in range(4):
                        load_half(sp, ph, w_ada[layer, i * 4 + j, :, :], i, 4, j)

            ada(0)
            for j in range(RAW):
                load_half(sp, "kv", w_in0[j, :, :], 0, 0, j)
            sp.wait_ge(sem("h_lo"), KT)
            sp.dma_start(mc, mixc).then_inc(sem("mix_in"), 16)
            sp.dma_start(sgub[0:1, :], sgu_b).then_inc(sem("mix_in"), 16)
            for j in range(RAW, 4 * KVH):
                load_half(sp, "kv", w_in0[j, :, :], 0, 0, j)
            PER = 20
            with sp.Fori(0, GROUPS // 2) as i:
                for j in range(PER):
                    load_half(sp, "mix", w_in0[i * PER + (4 * KVH + j), :, :], i, PER, j)
            load_half(sp, "out0", w_out0[0, :, :], 0, 0, 0)
            for j in range(1, 4):
                load_half(sp, "out0", w_out0[j, :, :], 0, 0, j)
            sp.wait_ge(sem("merged_lo"), KT)
            sp.dma_start(xres, xT.rearrange("p (k t) -> p k t", t=T)).then_inc(sem("xres_in"), 16)
            with sp.Fori(1, 8) as i:
                for j in range(4):
                    load_half(sp, "out0", w_out0[i * 4 + j, :, :], i, 4, j)
            ada(1)
            for j in range(2):
                load_half(sp, "ba", w_in1[j, :, :], 0, 0, j)
            sp.wait_ge(sem("x1_ready"), 2 * KT)
            sp.dma_start(keep_x1, xv[:, :, SEG:T]).then_inc(sem("x1_kept"), 16)
            with sp.Fori(0, KH) as i:
                for j in range(12):
                    load_half(sp, "delta", w_in1[i * 12 + (2 + j), :, :], i, 12, j)
            for j in range(4):
                load_half(sp, "out1", w_out1[j, :, :], 0, 0, j)
            sp.wait_ge(sem("y_ready"), KH + 1)
            sp.wait_ge(sem("x1_kept"), 16)
            sp.dma_start(x1, keep_x1).then_inc(sem("x1_back"), 16)
            with sp.Fori(1, 16) as i:
                for j in range(4):
                    load_half(sp, "out1", w_out1[i * 4 + j, :, :], i, 4, j)
            with sp.Fori(0, KT // 2) as i:
                for b in range(2):
                    sp.wait_ge(sem("f_scaled"), i * 2 + (b + 1))
                    sp.dma_start(out[i * 2 + b, :, :], f_out[b]).then_inc(sem(f"stored{b}"), 16)
            for b in range(2):
                sp.wait_ge(sem(f"stored{b}"), 8 * KT)

        @block.tensor
        def _(pe):
            begin(pe, "mixed", "attended", "scored", "o_done", "o_summed")

            def ada(layer):
                ph = f"ada{layer}"
                pe.wait_ge(sem("sil_ready"), 1)
                with pe.Fori(0, 24) as i:
                    for j in range(4):
                        pe.wait_ge(loaded[j], slot_loads(ph, i, 4, j))
                        if j == 0:
                            pe.wait_ge(sem("ada_read"), i + 24 * layer + 1)
                        for k in range(HALF):
                            kk = (j % 2) * HALF + k
                            done = pe.matmul(pb[7][:, 2 * (j // 2):2 * (j // 2) + 2], wins[j][:, k, :],
                                             silc[:, 2 * kk:2 * kk + 2], start=(kk == 0), stop=(kk == KT - 1))
                        done.then_inc(half_done, 1)

            def square_sum(layer):
                for k in range(KT):
                    pe.wait_ge(sem("n_squared"), layer * KT + k + 1)
                    pe.matmul(pb[6][:, :], ones[:, :], n_sq[k % 2], start=(k == 0), stop=(k == KT - 1))\
                      .then_inc(sem("n_summed"), 1)

            pe.wait_ge(sem("small_in"), 32)
            pe.wait_ge(sem("consts"), 3)
            square_sum(0)
            ada(0)

            pe.wait_ge(sem("h_lo"), KT)
            pe.wait_ge(sem("mix_in"), 32)
            for n in range(2 * KVH):
                b = n % 2
                if n >= 2:
                    pe.wait_ge(sem("kv_copied"), n - 1)
                tile(pe, "kv", 0, 0, n, pb[b][:, :])
            for g in range(KVH):
                pe.wait_ge(sem("k_squared"), g + 1)
                if g:
                    pe.wait_ge(sem("k_root"), g)
                pe.matmul(pb[3][:, :], ones[:, :], a_sq, start=True, stop=True).then_inc(sem("k_summed"), 1)
                pe.wait_ge(sem("k_normed"), g + 1)
                pe.matmul(pb[4][:, 0:SEG], mc[:, MO["rot"][0]:MO["rot"][1]], kTa[:, g * T + SEG:(g + 1) * T],
                          start=True, stop=True).then_inc(sem("k_rotated"), 1)
            for g in range(KVH):
                pe.wait_ge(sem("kv_copied"), KVH + g + 1)
                for t in range(NT):
                    done = pe.transpose(pb[5 + g][:, t * P:(t + 1) * P],
                                        [a_vT, a_ug][g][:, t * P:(t + 1) * P], ident)
                done.then_inc(sem("vv_turned"), 1)
            pe.wait_ge(sem("vv_ready"), KVH)
            pe.wait_ge(sem("k_ready"), KVH)

            ROT = mc[:, MO["rot"][0]:MO["rot"][1]]
            PER = 20

            def step(kv, i, b, n):
                j0 = 5 * b
                pe.wait_ge(sem("q_copied"), n + 1)
                pe.wait_ge(sem("ug_ready"), n + 1)
                tile(pe, "mix", i, PER, j0, pb[0][:, :])
                pe.wait_ge(sem("ga_read"), n + 1)
                tile(pe, "mix", i, PER, j0 + 1, pb[1][:, :])
                pe.wait_ge(sem("q_squared"), n + 1)
                pe.wait_ge(sem("pt_copied"), n * 3 + 1)
                pe.matmul(pb[3][:, :], ones[:, :], a_sq, start=True, stop=True).then_inc(sem("q_summed"), 1)
                tile(pe, "mix", i, PER, j0 + 2, pb[0][:, :])
                pe.wait_ge(sem("q_normed"), n + 1)
                pe.matmul(pb[4][:, 0:SEG], ROT, a_q[:, SEG:T], start=True, stop=True).then_inc(sem("q_rotated"), 1)
                pe.wait_ge(sem("v_copied"), n + 1)
                pe.wait_ge(sem("a_merged"), n + 1)
                for t in range(NT):
                    done = pe.transpose(pb[5][:, t * P:(t + 1) * P], a_vT[:, t * P:(t + 1) * P], ident)
                done.then_inc(sem("v_turned"), 1)
                tile(pe, "mix", i, PER, j0 + 3, pb[1][:, :])
                pe.wait_ge(sem("q_ready"), n + 1 + 1)
                for t in range(NT):
                    dst = pb[6][:, t * SEG:(t + 1) * SEG] if t < 2 else pb[1 + t][:, :]
                    done = pe.matmul(dst, a_q[:, t * P:(t + 1) * P],
                                     kTa[:, kv * T:kv * T + (SEG if t < 2 else T)], start=True, stop=True)
                    if t:
                        done.then_inc(sem("scored"), 1)
                pe.wait_ge(sem("vn_ready"), n + 1)
                rep = sgub[0:1, bass.ds(n * P, P)].rearrange("p (o n) -> p o n", o=1).to_broadcast([1, NT, P])
                pe.matmul(pb[5][:, :].rearrange("p (t n) -> p t n", n=P), ones[0:1, :], rep, start=True, stop=False)
                for t in range(NT):
                    done = pe.matmul(pb[5][:, t * P:(t + 1) * P], a_vn[:, t * P:(t + 1) * P],
                                     mc[:, bass.ds(n * P, P)], start=False, stop=(t == NT - 1))
                done.then_inc(sem("mixed"), 1)
                pe.wait_ge(sem("gb_read"), n + 1)
                tile(pe, "mix", i, PER, j0 + 4, pb[2][:, :])
                pe.wait_ge(sem("p_ready"), (n + 1) * 4)
                for t in range(2):
                    for s in range(2):
                        done = pe.transpose(pb[6][:, s * SEG + t * P:s * SEG + (t + 1) * P],
                                            a_p[:, t * SEG + s * P:t * SEG + (s + 1) * P], ident)
                done.then_inc(sem("p_turned"), 1)
                for sp_ in range(2):
                    for t in range(2):
                        for s in range(2):
                            done = pe.transpose(
                                pb[3 + sp_][:, s * SEG + t * P:s * SEG + (t + 1) * P],
                                a_p[:, T + t * T + (2 * sp_ + s) * P:T + t * T + (2 * sp_ + s + 1) * P], ident)
                    done.then_inc(sem("p_turned"), 1)
                pe.wait_ge(sem("b_merged"), n + 1)
                pe.wait_ge(sem("pt_copied"), (n + 1) * 3 + 1)
                for s in range(2):
                    pe.matmul(pb[7][:, 0:SEG], vva[:, kv * T + s * P:kv * T + (s + 1) * P],
                              a_pt[:, s * SEG:(s + 1) * SEG], start=(s == 0), stop=(s == 1))
                for s in range(NT):
                    done = pe.matmul(pb[7][:, SEG:T], vva[:, kv * T + s * P:kv * T + (s + 1) * P],
                                     a_pt[:, (2 + s) * SEG:(3 + s) * SEG], start=(s == 0), stop=(s == NT - 1))
                done.then_inc(sem("attended"), 1)

            for kv in range(KVH):
                with pe.Fori(2 * kv, 2 * kv + 2) as i:
                    for b in range(2):
                        step(kv, i, b, i * 2 + b)

            pe.wait_ge(sem("merged_lo"), KT)
            for b in range(2):
                tile(pe, "out0", 0, 4, b, pb[b][:, :])
            with pe.Fori(1, 8) as i:
                for b in range(2):
                    pe.wait_ge(sem("x1_ready"), i * 4 + (2 * b - 2))
                    tile(pe, "out0", i, 4, b, pb[b][:, :])

            square_sum(1)
            ada(1)

            pe.wait_ge(sem("h_lo"), 2 * KT)
            tile(pe, "ba", 0, 0, 0, pb[0][:, :])
            pe.wait_ge(sem("ba_copied"), 1)
            for t in range(NT):
                done = pe.transpose(pb[1][:, t * P:(t + 1) * P], b_fm[:, t * P:(t + 1) * P], ident)
            done.then_inc(sem("ba_turned"), 1)
            pe.wait_ge(sem("g_ready"), 1)
            gv = colv[:, G_ * 8:G_ * 8 + 8, :].rearrange("p (c d) h -> p c d h", d=2)
            for c in range(NT):
                for dr in range(2):
                    o = (c * 2 + dr) * VH
                    tri = sm[:, SO["tri"][0] + dr * P:SO["tri"][0] + (dr + 1) * P]
                    pe.matmul(pb[2][:, o:o + VH], tri, gv[:, c, dr, :], start=True, stop=True)
                    done = pe.matmul(pb[3][:, o:o + VH], ones[:, :], gv[:, c, dr, :], start=True, stop=True)
            done.then_inc(sem("g_summed"), 1)

            pe.wait_ge(sem("identr_ready"), 2)

            def chunk(t, dr):
                return [0, 1, 2, 3][t] if dr == 0 else [1, 0, 3, 2][t]

            with pe.Fori(0, KH) as i:
                PER = 12

                def spread(c, bank, done_name):
                    for u in range(4):
                        tri = sm[:, SO["tri"][0] + (u // 2) * P:SO["tri"][0] + (u // 2 + 1) * P]
                        done = pe.matmul(pb[bank][:, u * P:(u + 1) * P], col(G_, c, u).to_broadcast([P, P]), tri,
                                         start=True, stop=True)
                    done.then_inc(sem(done_name), 1)

                def half(j, ps, t0, t1):
                    b = j % 2
                    project(pe, "delta", i, PER, j, ps, lambda k: hhv[:, b * HALF + k, t0:t1],
                            lambda k: hlv[:, b * HALF + k, t0:t1], b == 0, b == 1)

                pe.wait_ge(sem("z_done"), i * 2 + 1)
                tile(pe, "delta", i, PER, 0, pb[0][:, :])
                pe.wait_ge(sem("cols_ready"), i + 1)
                pe.wait_ge(sem("o_normed"), i + 1)
                for c in range(NT):
                    spread(c, 2 + c, "gc_spread")
                tile(pe, "delta", i, PER, 1, pb[1][:, 0:SEG], SEG, T)
                pe.wait_ge(sem("dk_squared"), i + 1)
                pe.matmul(pb[6][:, :], ones[:, :], d_sq, start=True, stop=True).then_inc(sem("dk_summed"), 1)
                pe.wait_ge(sem("conv_done"), i * 4 + 1)
                tile(pe, "delta", i, PER, 2, pb[0][:, :])
                pe.wait_ge(sem("dq_squared"), i + 1)
                pe.matmul(pb[7][:, 0:SEG], ones[:, :], d_sq[:, 0:SEG], start=True, stop=True)\
                  .then_inc(sem("dq_summed"), 1)
                pe.wait_ge(sem("dk_ready"), i + 1)
                for c in range(NT):
                    done = pe.transpose(pb[6][:, c * P:(c + 1) * P], kT[:, c * P:(c + 1) * P], ident)
                done.then_inc(sem("k_turned"), 1)
                pe.wait_ge(sem("dq_root"), i + 1)
                for c in range(NT):
                    done = pe.matmul(pb[7][:, c * P:(c + 1) * P], kT[:, c * P:(c + 1) * P], kT[:, c * P:(c + 1) * P],
                                     start=True, stop=True)
                done.then_inc(sem("kk_done"), 1)
                pe.wait_ge(sem("dq_ready"), i + 1)
                pe.wait_ge(sem("gc_read"), (i + 1) * 4)
                for c in range(2):
                    done = pe.matmul(pb[2][:, c * P:(c + 1) * P], kT[:, (2 + c) * P:(3 + c) * P],
                                     qT[:, c * P:(c + 1) * P], start=True, stop=True)
                done.then_inc(sem("kq_done"), 1)
                pe.wait_ge(sem("conv_done"), i * 4 + 2)
                tile(pe, "delta", i, PER, 3, pb[1][:, :])

                def two(bank):
                    pe.matmul(u4(pb[bank][:, :]), identr, over4(twice), start=True, stop=False)

                def x_step(l, c):
                    n = (l - 1) * 4 + c
                    pe.wait_ge(sem("m_merged"), i * 28 + (n + 1))
                    if n >= 2:
                        pe.wait_ge(sem("x_copied"), i * 24 + (n - 1))
                    else:
                        pe.wait_ge(sem("dv_copied"), (i + 1) * 2)
                    two(2 + c % 2)
                    for u in range(4):
                        done = pe.matmul(pb[2 + c % 2][:, u * P:(u + 1) * P], CR[c][:, u * P:(u + 1) * P],
                                         M[c][:, u * P:(u + 1) * P], start=False, stop=(u == 3))
                    done.then_inc(sem("x_done"), 1)

                def z_step(l, c):
                    n = l * 4 + c
                    if l == 0:
                        pe.wait_ge(sem("ct_ready"), i * 4 + (c + 1))
                    else:
                        pe.wait_ge(sem("x_copied"), i * 24 + (n - 3))
                        pe.wait_ge(sem("p_merged"), i * 28 + (n - 3))
                    if n >= 2:
                        pe.wait_ge(sem("m_merged"), i * 28 + (n - 1))
                    if l == 0:
                        two(4 + c % 2)
                    for u in range(4):
                        done = pe.matmul(pb[4 + c % 2][:, u * P:(u + 1) * P],
                                         (PI if l else CR)[c][:, u * P:(u + 1) * P],
                                         X1[c][:, u * P:(u + 1) * P] if l else identr, start=(l > 0),
                                         stop=(l > 0 or u == 3))
                    done.then_inc(sem("z_made"), 1)
                    if n >= 2:
                        pe.wait_ge(sem("p_merged"), i * 28 + (n - 1))
                    else:
                        pe.wait_ge(sem("kk_read"), i + 1)
                        pe.wait_ge(sem("ktok_ready"), i + 1)
                    if l == 0:
                        two(6 + c % 2)
                        done = pe.matmul(pb[6 + c % 2][:, :], identr, CR[c], start=False, stop=True)
                    else:
                        for u in range(4):
                            done = pe.matmul(pb[6 + c % 2][:, u * P:(u + 1) * P], X1[c][:, u * P:(u + 1) * P],
                                             PI[c][:, u * P:(u + 1) * P], start=True, stop=True)
                    done.then_inc(sem("zp_made"), 1)

                def refine_f(c):
                    pe.wait_ge(sem("m_merged"), i * 28 + (24 + c + 1))
                    pe.wait_ge(sem("x_copied"), i * 24 + (22 + c + 1 if c < 2 else 24))
                    if c >= 2:
                        pe.wait_ge(sem("g_made"), i * 4 + (c - 1))
                    for u in range(4):
                        done = pe.matmul(pb[2 + c % 2][:, u * P:(u + 1) * P], CT[c][:, u * P:(u + 1) * P],
                                         M[c][:, u * P:(u + 1) * P].bitcast(F32), start=True, stop=True)
                    done.then_inc(sem("f_made"), 1)

                def refine_h(c):
                    pe.wait_ge(sem("g_made"), i * 4 + (c + 1))
                    pe.wait_ge(sem("p_merged"), (i + 1) * 28)
                    if c >= 2:
                        pe.wait_ge(sem("pf_ready"), i * 4 + (c - 1))
                    for u in range(4):
                        done = pe.matmul(pb[6 + c % 2][:, u * P:(u + 1) * P], X1[c][:, u * P:(u + 1) * P],
                                         PI[c][:, u * P:(u + 1) * P], start=True, stop=True)
                    done.then_inc(sem("h_made"), 1)

                for c in range(NT):
                    z_step(0, c)
                pe.wait_ge(sem("kq_read"), i + 1)
                for v in range(2):
                    pe.wait_ge(sem("v_silu"), (i * 2) + v + 1)
                    for c in range(NT):
                        done = pe.transpose(pb[2 + v][:, c * P:(c + 1) * P], acc[v][:, c * P:(c + 1) * P], ident)
                    done.then_inc(sem("dv_turned"), 1)
                for l in range(1, LEVELS):
                    for c in range(NT):
                        x_step(l, c)
                    if l == 2:
                        pe.wait_ge(sem("conv_done"), i * 4 + 3)
                        half(8, pb[0][:, 0:SEG], SEG, T)
                    if l == 4:
                        half(9, pb[0][:, 0:SEG], SEG, T)
                    for c in range(NT):
                        z_step(l, c)
                for c in range(NT):
                    refine_f(c)
                for c in range(2):
                    spread(2 + c, 4 + c, "gc_again")
                for c in range(NT):
                    refine_h(c)

                def scan(t):
                    if t:
                        pe.wait_ge(sem("s_ready"), i * 3 + t)
                        for dr in range(2):
                            c = chunk(t, dr)
                            done = pe.matmul(pb[2][:, dr * SEG:(dr + 1) * SEG], kT[:, c * P:(c + 1) * P],
                                             SR[t - 1][:, dr * SEG:(dr + 1) * SEG], start=True, stop=True)
                        done.then_inc(sem("ks_done"), 1)
                        pe.wait_ge(sem("r_ready"), i * 3 + t)
                        if t == 3:
                            pe.wait_ge(sem("vo_ready"), i * 2 + 1)
                    else:
                        pe.wait_ge(sem("pf_ready"), (i + 1) * 4)
                    for u in range(4):
                        c = chunk(t, u // 2)
                        rhs = SR[3][:, u * P:(u + 1) * P] if t else vtok[u % 2][:, c * P:(c + 1) * P]
                        done = pe.matmul(pb[3][:, u * P:(u + 1) * P], PF[c][:, u * P:(u + 1) * P], rhs,
                                         start=True, stop=True)
                    done.then_inc(sem("vn_done"), 1)

                def update(t):
                    pe.wait_ge(sem("vk_ready"), i * 3 + (t + 1))
                    for dr in range(2):
                        c = chunk(t, dr)
                        done = pe.matmul(pb[7][:, dr * SEG:(dr + 1) * SEG], ktok[:, c * P:(c + 1) * P],
                                         VN[2][:, dr * SEG:(dr + 1) * SEG], start=True, stop=True)
                    done.then_inc(sem("su_done"), 1)

                scan(0)
                pe.wait_ge(sem("conv_done"), (i + 1) * 4)
                for b in range(2):
                    half(10 + b, pb[1][:, 0:SEG], SEG, T)
                    update(b)
                    scan(b + 1)
                update(2)
                scan(3)
                pe.wait_ge(sem("vo_ready"), (i + 1) * 2)
                pe.wait_ge(sem("qg_ready"), (i + 1) * 2)
                pe.wait_ge(sem("attn_ready"), (i + 1) * 2)
                for v in range(2):
                    for c in range(2):
                        o = v * SEG + c * P
                        for dr in range(2):
                            t = 2 + (c if dr == 0 else 1 - c)
                            u = 2 * dr + v
                            pe.matmul(pb[5][:, o:o + P], SR[t - 1][:, u * P:(u + 1) * P],
                                      QG[c][:, u * P:(u + 1) * P], start=(dr == 0), stop=False)
                            done = pe.matmul(pb[5][:, o:o + P], VN[t - 2][:, u * P:(u + 1) * P],
                                             attn[c][:, u * P:(u + 1) * P], start=False, stop=(dr == 1))
                done.then_inc(sem("o_done"), 1)
                pe.wait_ge(sem("o_squared"), i + 1)
                pe.matmul(pb[6][:, :], ones[:, :], d_sq, start=True, stop=True).then_inc(sem("o_summed"), 1)

            pe.wait_ge(sem("y_lo"), KT)
            def out_tile(i, b):
                for j in range(4):
                    project(pe, "out1", i, 8, 4 * b + j, pb[b][:, 0:SEG],
                            lambda k: hhy[:, j * HALF + k, :], lambda k: hly[:, j * HALF + k, :], j == 0, j == 3)

            for b in range(2):
                out_tile(0, b)
            with pe.Fori(1, 8) as i:
                for b in range(2):
                    pe.wait_ge(sem("x2_ready"), i * 2 + (b - 1))
                    out_tile(i, b)
            for k in range(KT):
                pe.wait_ge(sem("f_squared"), k + 1)
                pe.matmul(pb[2][:, 0:SEG], ones[:, :], f_sq[k % 2], start=(k == 0), stop=(k == KT - 1))\
                  .then_inc(sem("f_summed"), 1)

        @block.scalar
        def _(act):
            ch = Chain(act, sem("act_step"))
            begin(act, "ga_read", "gb_read", "pt_copied", "q_copied", "z_done")

            def norm_squares(layer):
                for k in range(KT):
                    if k >= 2:
                        act.wait_ge(sem("n_summed"), layer * KT + k - 1)
                    act.activation(n_sq[k % 2], xv[:, k, :], ACT.Square).then_inc(sem("n_squared"), 1)

            def norm_root(layer):
                act.wait_ge(sem("n_summed"), (layer + 1) * KT)
                act.activation(n_rinv, pb[6][:, :], ACT.Sqrt, scale=1.0 / D, bias=eps[:, 0:1])\
                   .then_inc(sem("n_root"), 1)

            def norm_affine(layer):
                act.wait_ge(sem("aff_ready"), layer + 1)
                if layer == 1:
                    act.wait_ge(sem("x1_kept"), 16)
                for k in range(KT):
                    act.wait_ge(sem("n_scaled"), layer * KT + k + 1)
                    if k >= 2:
                        act.wait_ge(sem("h_lo"), layer * KT + k - 1)
                    for s in range(2):
                        last = act.activation(n_full[k % 2][:, s * SEG:(s + 1) * SEG],
                                              n_t[k % 2][:, s * SEG:(s + 1) * SEG],
                                              ACT.Identity, scale=affa[:, k, s:s + 1], bias=mod[:, k, s:s + 1])
                        ch.link(last)
                    act.activation(hhv[:, k, :], n_full[k % 2], ACT.Copy).then_inc(sem("h_hi"), 1)

            act.wait_ge(sem("small_in"), 32)
            act.wait_ge(sem("consts"), 3)
            act.activation(silc[:, :], smc("cond"), ACT.Silu).then_inc(sem("sil_ready"), 1)
            act.wait_ge(sem("x_in"), 16)
            norm_squares(0)
            norm_root(0)
            norm_affine(0)

            act.wait_ge(sem("h_lo"), KT)
            act.wait_ge(sem("mix_in"), 32)
            for n in range(2 * KVH + 1):
                if n < 2 * KVH:
                    for b in range(2):
                        split_hi(act, "kv", 0, 0, 2 * n + b)
                if n:
                    act.wait_ge(half_done, tile_done("kv", 0, 0, n - 1))
                    dst = [kTa[:, 0:T], kTa[:, T:2 * T], a_vT, a_ug][n - 1]
                    act.activation(dst, pb[(n - 1) % 2][:, :], ACT.Copy).then_inc(sem("kv_copied"), 1)
            for g in range(KVH):
                act.wait_ge(sem("kv_copied"), g + 1)
                if g:
                    act.wait_ge(sem("k_summed"), g)
                act.activation(a_sq, kTa[:, g * T:(g + 1) * T], ACT.Square).then_inc(sem("k_squared"), 1)
                act.wait_ge(sem("k_summed"), g + 1)
                if g:
                    act.wait_ge(sem("k_normed"), g)
                act.activation(a_rinv, pb[3][:, :], ACT.Sqrt, scale=1.0 / HD, bias=eps[:, 0:1])\
                   .then_inc(sem("k_root"), 1)
            for g in range(KVH):
                act.wait_ge(sem("vv_turned"), g + 1)
                act.activation(vva[:, g * T:(g + 1) * T], pb[5 + g][:, :], ACT.Copy).then_inc(sem("vv_ready"), 1)

            def mix_step(i, b, n):
                j0 = 10 * b
                PER = 20
                for j in range(2):
                    split_hi(act, "mix", i, PER, j0 + j)
                for j in range(2, 4):
                    split_hi(act, "mix", i, PER, j0 + j)
                    if j == 2:
                        act.wait_ge(half_done, tile_done("mix", i, PER, 5 * b))
                        act.wait_ge(sem("q_ready"), n + 1)
                        act.wait_ge(sem("scored"), n * 3 + 1)
                        act.activation(a_q, pb[0][:, :], ACT.Copy).then_inc(sem("q_copied"), 1)
                        act.activation(a_sq, pb[0][:, :], ACT.Square).then_inc(sem("q_squared"), 1)
                for j in range(4, 6):
                    split_hi(act, "mix", i, PER, j0 + j)
                    if j == 4:
                        act.wait_ge(half_done, tile_done("mix", i, PER, 5 * b + 1))
                        act.activation(a_vT, pb[1][:, :], ACT.Copy).then_inc(sem("v_copied"), 1)
                        act.wait_ge(sem("q_summed"), n + 1)
                        act.activation(a_rinv, pb[3][:, :], ACT.Sqrt, scale=1.0 / HD, bias=eps[:, 0:1])\
                           .then_inc(sem("q_root"), 1)
                for j in range(6, 8):
                    split_hi(act, "mix", i, PER, j0 + j)
                act.wait_ge(sem("v_var"), n + 1)
                act.activation(a_col[:, 8:12], a_col[:, 4:8], ACT.Sqrt, scale=1.0 / P, bias=eps[:, 1:2])\
                   .then_inc(sem("v_root"), 1)
                split_hi(act, "mix", i, PER, j0 + 8)
                act.wait_ge(half_done, tile_done("mix", i, PER, 5 * b + 3))
                act.wait_ge(sem("ug_ready"), n + 1)
                act.activation(a_ga, pb[1][:, :], ACT.Silu).then_inc(sem("ga_read"), 1)
                act.wait_ge(sem("max_ready"), n + 1)
                for t in range(NT):
                    src = pb[6][:, t * SEG:(t + 1) * SEG] if t < 2 else pb[1 + t][:, :]
                    dst = a_p[:, t * SEG:(t + 1) * SEG] if t < 2 else a_p[:, T + (t - 2) * T:T + (t - 1) * T]
                    act.activation(dst, src, ACT.Exp, bias=a_col[:, 20 + t:21 + t], scale=SCALE,
                                   accum_out=a_col[:, 24 + t:25 + t]).then_inc(sem("exp_done"), 1)
                split_hi(act, "mix", i, PER, j0 + 9)
                act.wait_ge(half_done, tile_done("mix", i, PER, 5 * b + 4))
                act.wait_ge(sem("b_merged"), n + 1)
                act.activation(a_gb, pb[2][:, :], ACT.Silu).then_inc(sem("gb_read"), 1)
                for s, bank in enumerate((6, 3, 4)):
                    act.wait_ge(sem("p_turned"), n * 3 + (s + 1))
                    if s == 0:
                        act.wait_ge(sem("attended"), n + 1)
                    act.activation(a_pt[:, s * T:(s + 1) * T], pb[bank][:, :], ACT.Copy).then_inc(sem("pt_copied"), 1)

            for kv in range(KVH):
                with act.Fori(2 * kv, 2 * kv + 2) as i:
                    for b in range(2):
                        mix_step(i, b, i * 2 + b)

            act.wait_ge(half_done, FIRST["out0"])
            act.wait_ge(sem("b_merged"), QH + 1)
            for k in range(KT):
                act.activation(hhv[:, k, :], xv[:, k, :], ACT.Copy).then_inc(sem("merged_hi"), 1)
            with act.Fori(0, 8) as i:
                for j in range(4):
                    split_hi(act, "out0", i, 4, j)
            act.wait_ge(sem("x1_ready"), 2 * KT)
            norm_squares(1)
            norm_root(1)
            norm_affine(1)
            act.wait_ge(sem("h_lo"), 2 * KT)
            for j in range(2):
                split_hi(act, "ba", 0, 0, j)
            act.wait_ge(half_done, FIRST["delta"])
            act.activation(b_fm, pb[0][:, :], ACT.Copy).then_inc(sem("ba_copied"), 1)
            act.wait_ge(sem("ba_split"), 1)
            ch.link(act.activation(b_t[2], b_t[1], ACT.Exp, scale=-1.0))
            ch.link(act.activation(b_t[3], b_t[2], ACT.Ln, bias=1.0))
            act.activation(b_t[5][:, 0:2 * VH], smc("a_log"), ACT.Exp).then_inc(sem("soft_ready"), 1)
            act.activation(colv[:, BETA * 8:BETA * 8 + 8, :], b_t[4].rearrange("p (r h) -> p r h", h=VH),
                           ACT.Sigmoid).then_inc(sem("beta_ready"), 1)
            act.wait_ge(sem("gc_ready"), 1)
            act.activation(b_t[0], colv[:, GC * 8:GC * 8 + 8, :].rearrange("p r h -> p (r h)"), ACT.Exp)\
               .then_inc(sem("gexp"), 1)
            act.activation(b_t[1], b_t[3], ACT.Exp).then_inc(sem("gexp"), 1)
            act.activation(colv[:, GL * 8:GL * 8 + 8, :].rearrange("p r h -> p (r h)"), pb[3][:, 0:SEG], ACT.Exp)\
               .then_inc(sem("gexp"), 1)

            act.activation(identr, ident, ACT.Copy).then_inc(sem("identr_ready"), 1)
            act.activation(twice, ident, ACT.Copy, scale=2.0).then_inc(sem("identr_ready"), 1)
            with act.Fori(0, KH) as i:
                PER = 12
                split_hi(act, "delta", i, PER, 0)
                split_hi(act, "delta", i, PER, 1)
                split_hi(act, "delta", i, PER, 2)
                act.wait_ge(sem("y_ready"), i + 1)
                for c in range(NT):
                    act.wait_ge(sem("gc_spread"), i * 4 + (c + 1))
                    for u in range(4):
                        last = act.activation(CT[c][:, u * P:(u + 1) * P], pb[2 + c][:, u * P:(u + 1) * P], ACT.Relu,
                                              scale=-1.0, bias=col(GC, c, u))
                    last.then_inc(sem("gc_read"), 1)
                    if c == 1:
                        split_hi(act, "delta", i, PER, 3)
                for c in range(NT):
                    act.wait_ge(sem("gc_read"), i * 4 + (c + 1))
                    act.activation(CT[c], CT[c], ACT.Exp, scale=-1.0).then_inc(sem("gc_exped"), 1)
                act.wait_ge(sem("conv_done"), i * 4 + 1)
                act.activation(kT, acc[0], ACT.Silu).then_inc(sem("dk_silu"), 1)
                act.wait_ge(sem("dk_silu"), i + 1)
                act.activation(d_sq, kT, ACT.Square).then_inc(sem("dk_squared"), 1)
                split_hi(act, "delta", i, PER, 4)
                act.wait_ge(sem("conv_done"), i * 4 + 2)
                act.activation(qT, acc[1][:, 0:SEG], ACT.Silu).then_inc(sem("dq_silu"), 1)
                act.wait_ge(sem("dk_summed"), i + 1)
                act.activation(d_rinv, pb[6][:, :], ACT.Sqrt, bias=eps[:, 0:1]).then_inc(sem("dk_root"), 1)
                act.wait_ge(sem("dq_silu"), i + 1)
                act.activation(d_sq[:, 0:SEG], qT, ACT.Square).then_inc(sem("dq_squared"), 1)
                split_hi(act, "delta", i, PER, 5)
                act.wait_ge(sem("dq_summed"), i + 1)
                act.wait_ge(sem("dk_ready"), i + 1)
                act.activation(d_rinv[:, 0:SEG], pb[7][:, 0:SEG], ACT.Sqrt, bias=eps[:, 0:1])\
                   .then_inc(sem("dq_root"), 1)
                split_hi(act, "delta", i, PER, 6)
                act.wait_ge(sem("k_turned"), i + 1)
                act.activation(ktok, pb[6][:, :], ACT.Copy).then_inc(sem("ktok_ready"), 1)
                act.wait_ge(sem("kq_done"), i + 1)
                act.activation(d_rinv[:, 0:SEG], pb[2][:, 0:SEG], ACT.Copy).then_inc(sem("kq_read"), 1)
                act.wait_ge(sem("conv_done"), i * 4 + 3)
                act.activation(acc[0], acc[0], ACT.Silu).then_inc(sem("v_silu"), 1)
                split_hi(act, "delta", i, PER, 7)
                act.wait_ge(sem("conv_done"), i * 4 + 4)
                act.activation(acc[1], acc[1], ACT.Silu).then_inc(sem("v_silu"), 1)
                split_hi(act, "delta", i, PER, 8)
                for v in range(2):
                    act.wait_ge(sem("dv_turned"), i * 2 + (v + 1))
                    act.activation(vtok[v], pb[2 + v][:, :], ACT.Copy).then_inc(sem("dv_copied"), 1)
                for l in range(1, LEVELS):
                    for c in range(NT):
                        act.wait_ge(sem("x_done"), i * 24 + ((l - 1) * 4 + c + 1))
                        act.activation(X1[c], pb[2 + c % 2][:, :], ACT.Copy).then_inc(sem("x_copied"), 1)
                    if l == 2:
                        split_hi(act, "delta", i, PER, 9)
                    if l == 4:
                        split_hi(act, "delta", i, PER, 10)
                act.wait_ge(half_done, i * PER + (FIRST["delta"] + 10))
                zi = xv[:, bass.ds(i, 1), :].rearrange("p o t -> p (o t)")
                act.activation(zi[:, 0:SEG], pb[0][:, 0:SEG], ACT.Silu).then_inc(sem("z_done"), 1)
                split_hi(act, "delta", i, PER, 11)
                for c in range(2):
                    act.wait_ge(sem("gc_again"), i * 2 + (c + 1))
                    act.wait_ge(sem("h_made"), (i + 1) * 4)
                    act.activation(QG[c], pb[4 + c][:, :], ACT.Exp).then_inc(sem("gc_exp"), 1)
                act.wait_ge(half_done, tile_done("delta", i, PER, 5))
                act.activation(zi[:, SEG:T], pb[1][:, 0:SEG], ACT.Silu).then_inc(sem("z_done"), 1)
                for t in range(2, NT):
                    act.wait_ge(sem("vn_done"), i * 4 + (t + 1))
                    if t == 2:
                        act.wait_ge(sem("vk_ready"), (i + 1) * 3)
                    for u in range(4):
                        c = t if u < 2 else 5 - t
                        last = act.activation(VN[t - 2][:, u * P:(u + 1) * P], pb[3][:, u * P:(u + 1) * P],
                                              ACT.Copy, scale=col(BETA, c, u))
                    last.then_inc(sem("vo_ready"), 1)
                act.wait_ge(sem("o_done"), i + 1 + 1)
                act.activation(d_sq, pb[5][:, :], ACT.Square).then_inc(sem("o_squared"), 1)
                act.wait_ge(sem("o_summed"), i + 1 + 1)
                act.activation(d_rinv, pb[6][:, :], ACT.Sqrt, scale=1.0 / HD, bias=eps[:, 0:1])\
                   .then_inc(sem("o_root"), 1)

            act.wait_ge(half_done, FIRST["out1"])
            act.wait_ge(sem("y_ready"), KH + 1)
            for k in range(KT):
                act.activation(hhv[:, k, :], xv[:, k, :], ACT.Copy).then_inc(sem("y_hi"), 1)
            with act.Fori(0, 16) as i:
                for j in range(4):
                    split_hi(act, "out1", i, 4, j)
            for k in range(KT):
                act.wait_ge(sem("x2_ready"), k + 1)
                if k >= 2:
                    act.wait_ge(sem("f_summed"), k - 1)
                act.activation(f_sq[k % 2], x1[:, k, :], ACT.Square).then_inc(sem("f_squared"), 1)
            act.wait_ge(sem("f_summed"), KT)
            act.activation(f_rinv, pb[2][:, 0:SEG], ACT.Sqrt, scale=1.0 / D, bias=eps[:, 0:1])\
               .then_inc(sem("f_root"), 1)

        @block.vector
        def _(dve):
            ch = Chain(dve, sem("dve_step"))
            begin(dve, "a_merged", "b_merged", "q_ready", "ug_ready", "ada_read", "o_normed", "y_ready")
            dve.memset(ones[:, :], 1.0).then_inc(sem("consts"), 1)
            dve.memset(eps[:, 0:1], EPS).then_inc(sem("consts"), 1)
            dve.memset(eps[:, 1:2], SGU_EPS).then_inc(sem("consts"), 1)
            dve.wait_ge(sem("small_in"), 32)
            dve.tensor_copy(mk[:, :], masks_in).then_inc(sem("masks_ready"), 1)
            dve.wait_ge(sem("masks_ready"), 1)

            def ada(layer):
                ph = f"ada{layer}"
                with dve.Fori(0, 24) as i:
                    dve.wait_ge(half_done, i * 4 + (FIRST[ph] + 4))
                    dve.tensor_tensor(
                        mod[:, bass.ds(i * 2, 2), :], pb[7][:, 0:4].rearrange("p (n c) -> p n c", c=2),
                        sm[:, bass.ds(i * 2 + (SO["ada_b"][0] + layer * 3 * KT), 2)]
                        .rearrange("p (n o) -> p n o", o=1).to_broadcast([P, 2, 2]), ALU.add)\
                       .then_inc(sem("ada_read"), 1)
                dve.wait_ge(sem("ada_read"), 24 * (layer + 1) + 1)
                ch.link(dve.tensor_scalar(affa[:, :, :], mod[:, KT:2 * KT, :], 1.0, None, ALU.add))
                nw = sm[:, SO["norm_w"][0] + layer * KT:SO["norm_w"][0] + (layer + 1) * KT]
                dve.tensor_tensor(affa[:, :, :], affa[:, :, :],
                                  nw.rearrange("p (k o) -> p k o", o=1).to_broadcast([P, KT, 2]),
                                  ALU.mult).then_inc(sem("aff_ready"), 1)

            def norm(layer):
                dve.wait_ge(sem("n_root"), layer + 1)
                ch.link(dve.reciprocal(n_rinv, n_rinv))
                ada(layer)
                for k in range(KT):
                    if k >= 2:
                        dve.wait_ge(sem("h_hi"), layer * KT + k - 1)
                    dve.tensor_tensor(n_t[k % 2], xv[:, k, :], n_rinv, ALU.mult).then_inc(sem("n_scaled"), 1)
                    if k >= 1:
                        lo(layer, k - 1)
                lo(layer, KT - 1)

            def lo(layer, k):
                dve.wait_ge(sem("h_hi"), layer * KT + k + 1)
                dve.tensor_tensor(hlv[:, k, :], n_full[k % 2], hhv[:, k, :].bitcast(F32), ALU.subtract)\
                   .then_inc(sem("h_lo"), 1)

            norm(0)

            def head_norm(dst, w, rooted, value, done):
                dve.wait_ge(sem(rooted), value)
                ch.link(dve.reciprocal(a_rinv, a_rinv))
                dve.scalar_tensor_tensor(out=dst, in0=dst, scalar=w, in1=a_rinv, op0=ALU.mult, op1=ALU.mult)\
                   .then_inc(sem(done), 1)

            def rope(dst, turned, value, done):
                dve.wait_ge(sem(turned), value)
                ch.link(dve.tensor_tensor(a_rot, pb[4][:, 0:SEG], mc[:, MO["sin"][0]:MO["sin"][1]], ALU.mult))
                ch.link(dve.tensor_tensor(dst, dst, mc[:, MO["cos"][0]:MO["cos"][1]], ALU.mult))
                dve.tensor_tensor(dst, dst, a_rot, ALU.add).then_inc(sem(done), 1)

            dve.wait_ge(sem("mix_in"), 32)
            for j in range(4 * KVH):
                split_lo(dve, "kv", 0, 0, j)
            for g in range(KVH):
                head_norm(kTa[:, g * T:(g + 1) * T], smc("k_w"), "k_root", g + 1, "k_normed")
                dve.wait_ge(sem("k_normed"), g + 1)
                rope(kTa[:, g * T + SEG:(g + 1) * T], "k_rotated", g + 1, "k_ready")

            MIX_LINKS = 2 * 12

            def mix_step(i, b, n):
                PER = 20
                j0 = 10 * b
                for j in range(4):
                    split_lo(dve, "mix", i, PER, j0 + j)
                dve.wait_ge(sem("q_copied"), n + 1 + 1)
                dve.wait_ge(sem("q_squared"), n + 1)
                split_lo(dve, "mix", i, PER, j0 + 4)
                head_norm(a_q, smc("q_w"), "q_root", n + 1, "q_normed")
                split_lo(dve, "mix", i, PER, j0 + 5)
                dve.wait_ge(sem("q_normed"), n + 1)
                rope(a_q[:, SEG:T], "q_rotated", n + 1, "q_ready")
                split_lo(dve, "mix", i, PER, j0 + 6)
                dve.wait_ge(sem("v_turned"), n + 1)
                v3 = pb[5][:, :].rearrange("p (t c) -> p t c", c=P)
                vn3 = a_vn.rearrange("p (t c) -> p t c", c=P)
                ch.link(dve.reduce_sum(a_col[:, 0:4], v3, axis=AX))
                ch.link(dve.tensor_scalar(a_col[:, 12:16], a_col[:, 0:4], 1.0 / P, None, ALU.mult))
                mean = a_col[:, 12:16].rearrange("p (t o) -> p t o", o=1).to_broadcast([P, NT, P])
                dve.wait_ge(sem("mixed"), n + 1)
                ch.link(dve.tensor_tensor(vn3, v3, mean, ALU.subtract))
                ch.link(dve.tensor_tensor(a_vsq, a_vn, a_vn, ALU.mult))
                dve.reduce_sum(a_col[:, 4:8], a_vsq.rearrange("p (t c) -> p t c", c=P), axis=AX)\
                   .then_inc(sem("v_var"), 1)
                split_lo(dve, "mix", i, PER, j0 + 7)
                dve.wait_ge(sem("v_root"), n + 1)
                ch.link(dve.reciprocal(a_col[:, 16:20], a_col[:, 8:12]))
                rstd = a_col[:, 16:20].rearrange("p (t o) -> p t o", o=1).to_broadcast([P, NT, P])
                dve.tensor_tensor(vn3, vn3, rstd, ALU.mult).then_inc(sem("vn_ready"), 1)
                split_lo(dve, "mix", i, PER, j0 + 8)
                dve.wait_ge(sem("ga_read"), n + 1 + 1)
                dve.tensor_tensor(a_ug, pb[0][:, :], a_ga, ALU.mult).then_inc(sem("ug_ready"), 1)
                dve.wait_ge(sem("scored"), n * 3 + 3 + 1)
                dve.reduce_max(a_col[:, 28:30], pb[6][:, :].rearrange("p (t s) -> p t s", s=SEG), axis=AX)
                dve.reduce_max(a_col[:, 30:31], pb[3][:, :], axis=AX)
                ch.link(dve.reduce_max(a_col[:, 31:32], pb[4][:, :], axis=AX))
                dve.tensor_scalar(a_col[:, 20:24], a_col[:, 28:32], -SCALE, None, ALU.mult)\
                   .then_inc(sem("max_ready"), 1)
                dve.wait_ge(sem("mixed"), n + 1 + 1)
                dve.wait_ge(sem("ug_ready"), n + 1 + 1)
                dve.tensor_tensor(xv[:, bass.ds(n, 1), :].rearrange("p o t -> p (o t)"), pb[5][:, :], a_ug, ALU.mult)\
                   .then_inc(sem("a_merged"), 1)
                dve.wait_ge(sem("exp_done"), (n + 1) * 4)
                ch.link(dve.reciprocal(a_col[:, 32:36], a_col[:, 24:28]))
                for t in range(NT):
                    pr = a_p[:, t * SEG:(t + 1) * SEG] if t < 2 else a_p[:, T + (t - 2) * T:T + (t - 1) * T]
                    dve.tensor_scalar(pr, pr, a_col[:, 32 + t:33 + t], None, ALU.mult).then_inc(sem("p_ready"), 1)
                split_lo(dve, "mix", i, PER, j0 + 9)
                dve.wait_ge(sem("gb_read"), n + 1 + 1)
                dve.wait_ge(sem("attended"), n + 1 + 1)
                dve.tensor_tensor(xv[:, bass.ds(n + GROUPS, 1), :].rearrange("p o t -> p (o t)"),
                                  pb[7][:, :], a_gb, ALU.mult).then_inc(sem("b_merged"), 1)

            for kv in range(KVH):
                with dve.Fori(2 * kv, 2 * kv + 2) as i:
                    ch.start(i - 2 * kv if kv else i, 2 * 10)
                    for b in range(2):
                        mix_step(i, b, i * 2 + b)
                ch.end(2)

            dve.wait_ge(half_done, FIRST["out0"])
            for k in range(KT):
                dve.wait_ge(sem("merged_hi"), k + 1)
                dve.tensor_tensor(hlv[:, k, :], xv[:, k, :], hhv[:, k, :].bitcast(F32), ALU.subtract)\
                   .then_inc(sem("merged_lo"), 1)
            dve.wait_ge(sem("merged_lo"), KT)
            with dve.Fori(0, 8) as i:
                for j in range(4):
                    split_lo(dve, "out0", i, 4, j)
                dve.wait_ge(sem("xres_in"), 16)
                for b in range(2):
                    dve.wait_ge(half_done, i * 4 + (FIRST["out0"] + 2 * b + 2))
                    for s in range(2):
                        sl = slice(s * SEG, (s + 1) * SEG)
                        dve.scalar_tensor_tensor(
                            out=xv[:, bass.ds(i * 2 + b, 1), sl].rearrange("p o t -> p (o t)"), in0=pb[b][:, sl],
                            scalar=mod[:, bass.ds(i * 2 + (2 * KT + b), 1), s:s + 1].rearrange("p o t -> p (o t)"),
                            in1=xres[:, bass.ds(i * 2 + b, 1), sl].rearrange("p o t -> p (o t)"),
                            op0=ALU.mult, op1=ALU.add).then_inc(sem("x1_ready"), 1)
            dve.wait_ge(sem("x1_ready"), 2 * KT)
            norm(1)

            for j in range(2):
                split_lo(dve, "ba", 0, 0, j)
            dve.wait_ge(sem("ba_turned"), 1)
            ba = pb[1][:, :].rearrange("p (r k h) -> p r k h", k=2, h=VH)
            dtb = smc("dt_bias").rearrange("p (d h) -> p d h", h=VH)
            for c in range(NT):
                last = dve.tensor_tensor(b_t[0][:, c * 2 * VH:(c + 1) * 2 * VH].rearrange("p (d h) -> p d h", h=VH),
                                         ba[:, 2 * c:2 * c + 2, 1, :], dtb, ALU.add)
            ch.link(last)
            ch.link(dve.tensor_copy(b_t[4].rearrange("p (r h) -> p r h", h=VH), ba[:, :, 0, :]))
            dve.tensor_scalar(b_t[1], b_t[0], -1.0, None, ALU.mult)\
               .then_inc(sem("tmp_neg"), 1)
            dve.wait_ge(sem("tmp_neg"), 1)
            dve.tensor_tensor(b_t[1], b_t[0], b_t[1], ALU.max).then_inc(sem("ba_split"), 1)
            dve.wait_ge(sem("soft_ready"), 1)
            ch.link(dve.tensor_scalar(b_t[0], b_t[0], 0.0, None, ALU.max))
            ch.link(dve.tensor_tensor(b_t[3], b_t[3], b_t[0], ALU.add))
            ch.link(dve.tensor_scalar(b_t[5][:, 0:2 * VH], b_t[5][:, 0:2 * VH], -1.0, None, ALU.mult))
            for c in range(NT):
                done = dve.tensor_tensor(
                    colv[:, G_ * 8 + 2 * c:G_ * 8 + 2 * c + 2, :],
                    b_t[3][:, c * 2 * VH:(c + 1) * 2 * VH].rearrange("p (d h) -> p d h", h=VH),
                    b_t[5][:, 0:2 * VH].rearrange("p (d h) -> p d h", h=VH), ALU.mult)
            done.then_inc(sem("g_ready"), 1)
            dve.wait_ge(sem("g_summed"), 1)

            def flat(kind):
                return colv[:, kind * 8:kind * 8 + 8, :].rearrange("p r h -> p (r h)")

            ch.link(dve.tensor_copy(flat(GC), pb[2][:, 0:SEG]))
            dve.tensor_tensor(b_t[3], pb[3][:, 0:SEG], flat(GC), ALU.subtract).then_inc(sem("gc_ready"), 1)
            dve.wait_ge(sem("beta_ready"), 1)
            dve.wait_ge(sem("gexp"), 3)
            dve.tensor_scalar(flat(NBETA), flat(BETA), -1.0, None, ALU.mult)
            dve.tensor_scalar(flat(NEGC), b_t[0], -1.0, None, ALU.mult)
            ch.link(dve.tensor_tensor(flat(BEKD), flat(BETA), b_t[1], ALU.mult))

            def conv(dst, src, i, n, width):
                segs = width // SEG
                o3 = dst.rearrange("p (s t) -> p s t", t=SEG)
                i3 = src.rearrange("p (s t) -> p s t", t=SEG)

                def tap(k):
                    return sm[:, bass.ds(i * 20 + (SO["conv_w"][0] + n * 5 + k), 1)]
                ch.link(dve.tensor_scalar(dst, src, tap(2), None, ALU.mult))
                for k in (0, 1, 3, 4):
                    d = k - 2
                    a, b = max(0, -d), SEG - max(0, d)
                    ins = dve.scalar_tensor_tensor(out=o3[:, :, a:b], in0=i3[:, :, a + d:b + d], scalar=tap(k),
                                                   in1=o3[:, :, a:b], op0=ALU.mult, op1=ALU.add)
                    if k < 4:
                        ch.link(ins)
                ins.then_inc(sem("conv_done"), 1)

            MKV = mk[:, 0:3 * LEVELS * P].rearrange("p (l d n) -> p l d n", d=3, n=P)

            def mask(l, turned):
                return MKV[:, l, turned:turned + 2, :].rearrange("p d (o n) -> p d o n", o=1)\
                    .to_broadcast([P, 2, 2, P])

            off = mk[:, 3 * LEVELS * P:].rearrange("p (o n) -> p o n", o=1).to_broadcast([P, NT, P])
            def chunk(t, dr):
                return [0, 1, 2, 3][t] if dr == 0 else [1, 0, 3, 2][t]

            with dve.Fori(0, KH) as i:
                ch.start(i, 4 * 4 + 3)
                PER = 12
                dve.tensor_copy(ck.rearrange("p (r h) -> p r h", h=2), colv[:, :, bass.ds(i * 2, 2)])\
                   .then_inc(sem("cols_ready"), 1)
                split_lo(dve, "delta", i, PER, 0)
                split_lo(dve, "delta", i, PER, 2)
                dve.wait_ge(half_done, tile_done("delta", i, PER, 0))
                conv(acc[0], pb[0][:, :], i, 0, T)
                dve.wait_ge(half_done, tile_done("delta", i, PER, 1))
                conv(acc[1][:, 0:SEG], pb[1][:, 0:SEG], i, 1, SEG)
                split_lo(dve, "delta", i, PER, 4)
                dve.wait_ge(sem("dk_root"), i + 1)
                ch.link(dve.reciprocal(d_rinv, d_rinv))
                dve.tensor_tensor(kT, kT, d_rinv, ALU.mult).then_inc(sem("dk_ready"), 1)
                dve.wait_ge(sem("dq_root"), i + 1)
                ch.link(dve.reciprocal(d_rinv[:, 0:SEG], d_rinv[:, 0:SEG]))
                dve.scalar_tensor_tensor(out=qT, in0=qT, scalar=SCALE, in1=d_rinv[:, 0:SEG],
                                         op0=ALU.mult, op1=ALU.mult).then_inc(sem("dq_ready"), 1)
                dve.wait_ge(sem("kk_done"), i + 1)
                dve.tensor_tensor(u4(KK), u4(pb[7][:, :]), off, ALU.mult).then_inc(sem("kk_read"), 1)
                split_lo(dve, "delta", i, PER, 6)
                dve.wait_ge(half_done, tile_done("delta", i, PER, 2))
                dve.wait_ge(sem("dk_silu"), i + 1)
                conv(acc[0], pb[0][:, :], i, 2, T)
                dve.wait_ge(half_done, tile_done("delta", i, PER, 3))
                dve.wait_ge(sem("dq_silu"), i + 1)
                conv(acc[1], pb[1][:, :], i, 3, T)
                split_lo(dve, "delta", i, PER, 8)
                for l in range(LEVELS):
                    for c in range(NT):
                        for dst, bank, turned, made, done in ((M[c], 4, 0, "z_made", "m_merged"),
                                                              (PI[c], 6, 1, "zp_made", "p_merged")):
                            dve.wait_ge(sem(made), i * 28 + (l * 4 + c + 1))
                            if l < LEVELS - 1:
                                last = dve.tensor_tensor(q4(dst), q4(pb[bank + c % 2][:, :]), mask(l, turned), ALU.mult)
                            else:
                                last = dve.tensor_copy(dst, pb[bank + c % 2][:, :])
                            last.then_inc(sem(done), 1)
                    if l == 4:
                        split_lo(dve, "delta", i, PER, 10)
                for c in range(NT):
                    dve.wait_ge(sem("f_made"), i * 4 + (c + 1))
                    dve.tensor_tensor(X1[c], pb[2 + c % 2][:, :], M[c].bitcast(F32), ALU.subtract)\
                       .then_inc(sem("g_made"), 1)
                for c in range(NT):
                    dve.wait_ge(sem("h_made"), i * 4 + (c + 1))
                    dve.scalar_tensor_tensor(out=PF[c], in0=PI[c].bitcast(F32), scalar=2.0, in1=pb[6 + c % 2][:, :],
                                             op0=ALU.mult, op1=ALU.add).then_inc(sem("pf_ready"), 1)
                for t in range(NT):
                    if t:
                        dve.wait_ge(sem("ks_done"), i * 3 + t)
                        for u in range(4):
                            c = chunk(t, u // 2)
                            last = dve.scalar_tensor_tensor(
                                out=SR[3][:, u * P:(u + 1) * P], in0=pb[2][:, u * P:(u + 1) * P],
                                scalar=col(NEGC, c, u), in1=vtok[u % 2][:, c * P:(c + 1) * P],
                                op0=ALU.mult, op1=ALU.add)
                        last.then_inc(sem("r_ready"), 1)
                    if t < 3:
                        dve.wait_ge(sem("vn_done"), i * 4 + (t + 1))
                        for u in range(4):
                            c = chunk(t, u // 2)
                            last = dve.tensor_scalar(VN[2][:, u * P:(u + 1) * P], pb[3][:, u * P:(u + 1) * P],
                                                     col(BEKD, c, u), None, ALU.mult)
                        last.then_inc(sem("vk_ready"), 1)
                        dve.wait_ge(sem("su_done"), i * 3 + (t + 1))
                        if t == 0:
                            dve.tensor_copy(SR[0], pb[7][:, :]).then_inc(sem("s_ready"), 1)
                        else:
                            for u in range(4):
                                c = chunk(t, u // 2)
                                last = dve.scalar_tensor_tensor(
                                    out=SR[t][:, u * P:(u + 1) * P], in0=SR[t - 1][:, u * P:(u + 1) * P],
                                    scalar=col(GL, c, u), in1=pb[7][:, u * P:(u + 1) * P],
                                    op0=ALU.mult, op1=ALU.add)
                            last.then_inc(sem("s_ready"), 1)
                        if t < 2:
                            dve.wait_ge(sem("s_ready"), i * 3 + (t + 1))
                dve.wait_ge(sem("o_root"), i + 1)
                ch.link(dve.reciprocal(d_rinv, d_rinv))
                dve.scalar_tensor_tensor(out=d_sq, in0=pb[5][:, :], scalar=smc("o_w"), in1=d_rinv,
                                         op0=ALU.mult, op1=ALU.mult).then_inc(sem("o_normed"), 1)
                dve.wait_ge(sem("o_normed"), i + 1 + 1)
                dve.wait_ge(sem("z_done"), (i + 1) * 2 + 1)
                yi = xv[:, bass.ds(i, 1), :].rearrange("p o t -> p (o t)")
                dve.tensor_tensor(yi, yi, d_sq, ALU.mult).then_inc(sem("y_ready"), 1)
            ch.end(KH)

            dve.wait_ge(half_done, FIRST["out1"])
            for k in range(KT):
                dve.wait_ge(sem("y_hi"), k + 1)
                dve.tensor_tensor(hlv[:, k, :], xv[:, k, :], hhv[:, k, :].bitcast(F32), ALU.subtract)\
                   .then_inc(sem("y_lo"), 1)
            with dve.Fori(0, 8) as i:
                for b in range(2):
                    for j in range(4):
                        split_lo(dve, "out1", i, 8, 4 * b + j)
                    dve.wait_ge(sem("x1_back"), 16)
                    dve.wait_ge(half_done, i * 8 + (FIRST["out1"] + 4 * b + 4))
                    xt = x1[:, bass.ds(i * 2 + b, 1), :].rearrange("p o t -> p (o t)")
                    dve.scalar_tensor_tensor(
                        out=xt, in0=pb[b][:, 0:SEG],
                        scalar=mod[:, bass.ds(i * 2 + (2 * KT + b), 1), 1:2].rearrange("p o t -> p (o t)"),
                        in1=xt, op0=ALU.mult, op1=ALU.add).then_inc(sem("x2_ready"), 1)
            dve.wait_ge(sem("f_root"), 1)
            ch.link(dve.reciprocal(f_rinv, f_rinv))
            for k in range(KT):
                if k >= 2:
                    dve.wait_ge(sem(f"stored{k % 2}"), 16 * (k // 2))
                dve.scalar_tensor_tensor(out=f_out[k % 2], in0=x1[:, k, :], scalar=smc("final_w")[:, k:k + 1],
                                         in1=f_rinv, op0=ALU.mult, op1=ALU.mult).then_inc(sem("f_scaled"), 1)

        @block.gpsimd
        def _(pool):
            seen = smc("tri").rearrange("p (d o n) -> p d o n", d=2, o=1).to_broadcast([P, 2, 2, P])
            pool.wait_ge(sem("small_in"), 32)
            with pool.Fori(0, KH) as i:
                PER = 12
                split_lo(pool, "delta", i, PER, 1)
                split_lo(pool, "delta", i, PER, 3)
                for c in range(NT):
                    pool.wait_ge(sem("gc_exped"), i * 4 + (c + 1))
                    pool.tensor_tensor(q4(CT[c]), q4(CT[c]), seen, ALU.mult).then_inc(sem("decay_ready"), 1)
                split_lo(pool, "delta", i, PER, 5)
                pool.wait_ge(sem("kq_read"), i + 1)
                pool.wait_ge(sem("decay_ready"), (i + 1) * 4)
                for c in range(2):
                    pool.tensor_tensor(u4(attn[c]), u4(CT[2 + c]), over4(d_rinv[:, c * P:(c + 1) * P]), ALU.mult)\
                        .then_inc(sem("attn_ready"), 1)
                pool.wait_ge(sem("kk_read"), i + 1)
                pool.wait_ge(sem("attn_ready"), (i + 1) * 2)
                for c in range(NT):
                    pool.tensor_tensor(u4(CT[c]), u4(CT[c]), over4(KK[:, c * P:(c + 1) * P]), ALU.mult)\
                        .then_inc(sem("kk_times"), 1)
                    if c == 1:
                        split_lo(pool, "delta", i, PER, 7)
                for c in range(NT):
                    pool.wait_ge(sem("kk_times"), i * 4 + (c + 1))
                    pool.tensor_tensor(u4(CT[c]), u4(CT[c]), col4(NBETA, c), ALU.mult).then_inc(sem("ct_full"), 1)
                for c in range(NT):
                    pool.wait_ge(sem("ct_full"), i * 4 + (c + 1))
                    pool.tensor_tensor(u4(CR[c]), u4(CT[c]), over4(ident), ALU.subtract).then_inc(sem("ct_ready"), 1)
                split_lo(pool, "delta", i, PER, 9)
                split_lo(pool, "delta", i, PER, 11)
                for c in range(2):
                    pool.wait_ge(sem("gc_exp"), i * 2 + (c + 1))
                    pool.wait_ge(sem("dq_ready"), i + 1)
                    pool.tensor_tensor(u4(QG[c]), u4(QG[c]), over4(qT[:, c * P:(c + 1) * P]), ALU.mult)\
                        .then_inc(sem("qg_ready"), 1)


def halves(w):
    rows, cols = w.shape
    parts = rows // (HALF * P)
    t = w.reshape(parts, HALF, P, cols // P, P).transpose(3, 0, 2, 1, 4)
    return t.reshape(cols // P * parts, P, HALF * P)


def tokens_last(a):
    return a.T.reshape(KT, P, -1).transpose(1, 0, 2).reshape(P, -1)


def columns(v):
    return np.asarray(v).reshape(-1, P).T


def constants():
    r = np.arange(P)
    ident = np.eye(P, dtype=np.float32)
    tri = np.concatenate([r[:, None] <= r[None, :], r[:, None] >= r[None, :]], 1).astype(np.float32)
    lo = [((r[:, None] >> (l + 1)) == (r[None, :] >> (l + 1))) & (r[:, None] >= r[None, :]) for l in range(LEVELS)]
    masks = np.concatenate([m for l in lo for m in (l, l.T, l)] + [ident == 0], 1).astype(np.float32)
    axis = HD // 2
    row = np.repeat(np.arange(SEG // 64), 64).astype(np.float32)
    colm = np.tile(np.arange(64), SEG // 64).astype(np.float32)
    freqs = (np.float32(10000.0) ** (-np.arange(0, axis, 2, dtype=np.float32) / np.float32(axis))).astype(np.float32)
    ang = np.concatenate([row[:, None] * freqs, row[:, None] * freqs, colm[:, None] * freqs, colm[:, None] * freqs], 1)
    rot = np.zeros((P, P), np.float32)
    for h in range(2):
        for d in range(32):
            rot[h * 64 + 32 + d, h * 64 + d] = -1.0
            rot[h * 64 + d, h * 64 + 32 + d] = 1.0
    return ident, tri, masks, np.cos(ang).T.astype(np.float32), np.sin(ang).T.astype(np.float32), rot


def kernel(x, c, ctx, c_ctx, norm_w, ada_w, ada_b, ab_w_in, ab_w_out, sgu_w, sgu_b, q_norm_w, k_norm_w,
           dn_w_in, dn_conv_w, dn_a_log, dn_dt_bias, dn_norm_w, dn_w_out, final_norm_w):
    import concourse.bacc as bacc
    from concourse.bass_utils import run_bass_kernel_spmd

    c_all = lambda *a: np.ascontiguousarray(np.concatenate(a, 1))
    ident, tri, masks, cos, sin, rot = constants()
    xT = tokens_last(np.concatenate([ctx[0], x[0]], 0))
    cond = np.stack([columns(c_ctx), columns(c[0])], 2).reshape(P, 2 * KT)

    def spread(a):
        return np.broadcast_to(np.asarray(a).reshape(1, -1), (P, np.asarray(a).size))

    conv = np.asarray(dn_conv_w[0]).T.reshape(-1, P, 5)
    order = [t for h in range(KH) for t in (KH + h, h, 2 * KH + 2 * h, 2 * KH + 2 * h + 1)]
    conv = conv[order].transpose(1, 0, 2).reshape(P, -1)
    small = c_all(cond, columns(ada_b.reshape(-1)), columns(norm_w.reshape(-1)), columns(final_norm_w),
                  columns(q_norm_w[0]), columns(k_norm_w[0]), columns(dn_norm_w[0]), conv,
                  spread(dn_dt_bias[0]), spread(dn_a_log[0]), ident, tri)
    mixc = c_all(np.asarray(sgu_w[0]).transpose(2, 0, 1).reshape(P, -1), cos, sin, rot)

    h0 = halves(np.asarray(ab_w_in[0]))
    tiles0 = [32, 33, 34, 35] + [t for g in range(GROUPS) for t in (24 + g, 8 + g, g, 16 + g, 36 + g)]
    h0 = h0[[2 * t + b for t in tiles0 for b in range(2)]]
    h1 = halves(np.asarray(dn_w_in[0]))
    tiles1 = [96] + [t for h in range(KH) for t in (KH + h, h, 32 + 2 * h, 33 + 2 * h, 64 + 2 * h, 65 + 2 * h)]
    h1 = h1[[2 * t + b for t in tiles1 for b in range(2)]]
    arrays = {
        "xT": xT, "w_ada": np.stack([halves(np.asarray(ada_w[l])) for l in range(2)]), "w_in0": h0,
        "w_out0": halves(np.asarray(ab_w_out[0])), "w_in1": h1, "w_out1": halves(np.asarray(dn_w_out[0])),
        "small": small, "mixc": mixc, "sgu_b": np.asarray(sgu_b[0]).reshape(1, -1), "masks": masks,
    }
    arrays = {k: np.ascontiguousarray(v) for k, v in arrays.items()}
    nc = bacc.Bacc("TRN2", target_bir_lowering=False, num_devices=1)
    args = {k: nc.dram_tensor(k, v.shape, mybir.dt.from_np(v.dtype), kind="ExternalInput").ap()
            for k, v in arrays.items()}
    y = nc.dram_tensor("y", (KT, P, SEG), F32, kind="ExternalOutput").ap()
    keep = nc.dram_tensor("keep_x1", (P, KT, SEG), F32).ap()
    build(nc, out=y, keep_x1=keep, **args)
    r = run_bass_kernel_spmd(nc, [arrays], core_ids=[0])
    return r.results[0]["y"].reshape(D, SEG).T.reshape(1, SEG, D)
```
